# Optimizing a Trainium2 kernel written in Bass

```python
import jax, jax.numpy as jnp
from jax import lax
import numpy as np

D_MODEL = 1024
BATCH = 1
SEQ = 1024
DEPTH = 1
DEC_BATCH = 1
DEC_SEQ = 32
PAST_LEN = 128

CHUNK = 64
HEAD_DIM = 64
CONV_DIM = 256
CONV_K = 3
FOX_HEADS = 8
FOX_DIM = FOX_HEADS * HEAD_DIM
MEM_HEADS = 4
MEM_DIM = MEM_HEADS * HEAD_DIM
N_MEM = 256
MIX_DIM = CONV_DIM + FOX_DIM + MEM_DIM
IN_COLS = 3 * CONV_DIM + 3 * FOX_DIM + FOX_HEADS + MEM_DIM
D_FF = 2816
Q_BLOCK = 128
EPS = 1e-6
F32 = jnp.float32

kernel_name = 'hybrid_streaming_conv_fox_memory_step'

def _rmsnorm(x, g):
    xf = x.astype(F32)
    y = xf * lax.rsqrt(jnp.mean(xf * xf, axis=-1, keepdims=True) + EPS)
    return (y * g.astype(F32)).astype(x.dtype)

def _head_rms(x, g):
    return _rmsnorm(x, g)

def _swiglu(x, w_gate, w_up, w_down):
    return (jax.nn.silu(x @ w_gate) * (x @ w_up)) @ w_down

def _fox_attention(q, k, v, cum_q, cum_k, q_offset):
    bsz, tq, nh, dh = q.shape
    tk = k.shape[1]
    kpos = jnp.arange(tk)
    cum_k_t = jnp.swapaxes(cum_k, 1, 2)
    scale = dh ** -0.5

    def block(args):
        qb, cqb, qpos = args
        s = jnp.einsum('bqhd,bkhd->bhqk', qb, k).astype(F32) * scale
        s = s + jnp.swapaxes(cqb, 1, 2)[..., :, None] - cum_k_t[..., None, :]
        s = jnp.where(kpos[None, :] <= qpos[:, None], s, -jnp.inf)
        p = jax.nn.softmax(s, axis=-1)
        return jnp.einsum('bhqk,bkhd->bqhd', p.astype(v.dtype), v)

    qpos = q_offset + jnp.arange(tq)
    if tq <= Q_BLOCK:
        return block((q, cum_q, qpos))
    nb = tq // Q_BLOCK
    qb = q.reshape(bsz, nb, Q_BLOCK, nh, dh).transpose(1, 0, 2, 3, 4)
    cqb = cum_q.reshape(bsz, nb, Q_BLOCK, nh).transpose(1, 0, 2, 3)
    pb = qpos.reshape(nb, Q_BLOCK)
    out = lax.map(block, (qb, cqb, pb))
    return out.transpose(1, 0, 2, 3, 4).reshape(bsz, tq, nh, dh)

def _mem_attention(q, k, v):
    s = jnp.einsum('bqhd,bkhd->bhqk', q, k).astype(F32) * (HEAD_DIM ** -0.5)
    p = jax.nn.softmax(s, axis=-1)
    return jnp.einsum('bhqk,bkhd->bqhd', p.astype(v.dtype), v)

def _mem_kv(mem, g_mem, w_mem_kv, gk_mem):
    bsz, n, _ = mem.shape
    kv = _rmsnorm(mem, g_mem) @ w_mem_kv
    mk, mv = jnp.split(kv, [MEM_DIM], axis=-1)
    mk = _head_rms(mk.reshape(bsz, n, MEM_HEADS, HEAD_DIM), gk_mem)
    return mk, mv.reshape(bsz, n, MEM_HEADS, HEAD_DIM)

def _layer(x, conv_prev, past_k, past_v, past_logf, mem_k, mem_v, lp):
    (g_f1, w_g1, w_u1, w_d1, g_mix, w_in, b_f, conv_w, conv_b,
     gq_fox, gk_fox, gq_mem, w_out, g_f2, w_g2, w_u2, w_d2, g_fin) = lp
    bsz, t, _ = x.shape
    x = x + 0.5 * _swiglu(_rmsnorm(x, g_f1), w_g1, w_u1, w_d1)
    h = _rmsnorm(x, g_mix)
    proj = h @ w_in
    bounds = np.cumsum([CONV_DIM, CONV_DIM, CONV_DIM, FOX_DIM, FOX_DIM, FOX_DIM, FOX_HEADS]).tolist()
    u, c_gate, b_gate, q, k, v, f_logit, q_mem = jnp.split(proj, bounds, axis=-1)
    conv_in = c_gate * u
    padded = jnp.concatenate([conv_prev.astype(conv_in.dtype), conv_in], axis=1)
    conv = conv_b + conv_w[CONV_K - 1] * padded[:, CONV_K - 1:CONV_K - 1 + t]
    for i in range(CONV_K - 1):
        conv = conv + conv_w[i] * padded[:, i:i + t]
    y_conv = b_gate * conv
    new_conv = padded[:, t:]
    q = _head_rms(q.reshape(bsz, t, FOX_HEADS, HEAD_DIM), gq_fox)
    k = _head_rms(k.reshape(bsz, t, FOX_HEADS, HEAD_DIM), gk_fox)
    v = v.reshape(bsz, t, FOX_HEADS, HEAD_DIM)
    logf = jax.nn.log_sigmoid(f_logit.astype(F32) + b_f.astype(F32))
    p_len = past_k.shape[1]
    k_all = jnp.concatenate([past_k.astype(k.dtype), k], axis=1)
    v_all = jnp.concatenate([past_v.astype(v.dtype), v], axis=1)
    cum = jnp.cumsum(jnp.concatenate([past_logf.astype(F32), logf], axis=1), axis=1)
    y_fox = _fox_attention(q, k_all, v_all, cum[:, p_len:], cum, p_len)
    q_mem = _head_rms(q_mem.reshape(bsz, t, MEM_HEADS, HEAD_DIM), gq_mem)
    y_mem = _mem_attention(q_mem, mem_k.astype(q_mem.dtype), mem_v.astype(q_mem.dtype))
    mix = jnp.concatenate([y_conv, y_fox.reshape(bsz, t, FOX_DIM), y_mem.reshape(bsz, t, MEM_DIM)], axis=-1)
    x = x + mix @ w_out
    x = x + 0.5 * _swiglu(_rmsnorm(x, g_f2), w_g2, w_u2, w_d2)
    x = _rmsnorm(x, g_fin)
    return x, k, v, logf.astype(x.dtype), new_conv

def setup_inputs(seed: int = 0) -> dict:
    key = jax.random.key(seed)
    ks = jax.random.split(key, 32)

    def nrm(k, shape, scale=1.0):
        return jax.random.normal(k, shape, F32) * scale

    def gain(k, n):
        return 1.0 + 0.02 * jax.random.normal(k, (DEPTH, n), F32)

    return {
        'x_prompt': nrm(ks[0], (BATCH, SEQ, D_MODEL)),
        'x_sample': nrm(ks[1], (DEC_BATCH, DEC_SEQ, D_MODEL)),
        'cache_fox_k': nrm(ks[2], (DEPTH, DEC_BATCH, PAST_LEN, FOX_HEADS, HEAD_DIM)),
        'cache_fox_v': nrm(ks[3], (DEPTH, DEC_BATCH, PAST_LEN, FOX_HEADS, HEAD_DIM)),
        'cache_fox_logf': jax.nn.log_sigmoid(2.0 + nrm(ks[4], (DEPTH, DEC_BATCH, PAST_LEN, FOX_HEADS), 0.5)),
        'state_conv': nrm(ks[5], (DEPTH, DEC_BATCH, CONV_K - 1, CONV_DIM)),
        'cache_mem_k': nrm(ks[6], (DEPTH, DEC_BATCH, N_MEM, MEM_HEADS, HEAD_DIM)),
        'cache_mem_v': nrm(ks[7], (DEPTH, DEC_BATCH, N_MEM, MEM_HEADS, HEAD_DIM)),
        'mem_prompt': nrm(ks[8], (BATCH, N_MEM, D_MODEL)),
        'norm_ffn1': gain(ks[9], D_MODEL),
        'w_ffn1_gate': nrm(ks[10], (DEPTH, D_MODEL, D_FF), D_MODEL ** -0.5),
        'w_ffn1_up': nrm(ks[11], (DEPTH, D_MODEL, D_FF), D_MODEL ** -0.5),
        'w_ffn1_down': nrm(ks[12], (DEPTH, D_FF, D_MODEL), D_FF ** -0.5),
        'norm_mix': gain(ks[13], D_MODEL),
        'w_in': nrm(ks[14], (DEPTH, D_MODEL, IN_COLS), D_MODEL ** -0.5),
        'b_forget': 2.0 + nrm(ks[15], (DEPTH, FOX_HEADS), 0.5),
        'conv_w': nrm(ks[16], (DEPTH, CONV_K, CONV_DIM), CONV_K ** -0.5),
        'conv_b': nrm(ks[17], (DEPTH, CONV_DIM), 0.02),
        'q_norm_fox': gain(ks[18], HEAD_DIM),
        'k_norm_fox': gain(ks[19], HEAD_DIM),
        'q_norm_mem': gain(ks[20], HEAD_DIM),
        'k_norm_mem': gain(ks[21], HEAD_DIM),
        'norm_mem': gain(ks[22], D_MODEL),
        'w_mem_kv': nrm(ks[23], (DEPTH, D_MODEL, 2 * MEM_DIM), D_MODEL ** -0.5),
        'w_out': nrm(ks[24], (DEPTH, MIX_DIM, D_MODEL), MIX_DIM ** -0.5),
        'norm_ffn2': gain(ks[25], D_MODEL),
        'w_ffn2_gate': nrm(ks[26], (DEPTH, D_MODEL, D_FF), D_MODEL ** -0.5),
        'w_ffn2_up': nrm(ks[27], (DEPTH, D_MODEL, D_FF), D_MODEL ** -0.5),
        'w_ffn2_down': nrm(ks[28], (DEPTH, D_FF, D_MODEL), D_FF ** -0.5),
        'norm_final': gain(ks[29], D_MODEL),
    }

def reference(x_prompt, x_sample, cache_fox_k, cache_fox_v, cache_fox_logf, state_conv,
              cache_mem_k, cache_mem_v, mem_prompt,
              norm_ffn1, w_ffn1_gate, w_ffn1_up, w_ffn1_down, norm_mix, w_in, b_forget,
              conv_w, conv_b, q_norm_fox, k_norm_fox, q_norm_mem, k_norm_mem, norm_mem,
              w_mem_kv, w_out, norm_ffn2, w_ffn2_gate, w_ffn2_up, w_ffn2_down, norm_final):
    yp, ys = x_prompt, x_sample
    bp = x_prompt.shape[0]
    kp_l, vp_l, fp_l, cp_l, mkp_l, mvp_l = [], [], [], [], [], []
    ks_l, vs_l, fs_l, cs_l = [], [], [], []
    for l in range(DEPTH):
        lp = (norm_ffn1[l], w_ffn1_gate[l], w_ffn1_up[l], w_ffn1_down[l], norm_mix[l], w_in[l],
              b_forget[l], conv_w[l], conv_b[l], q_norm_fox[l], k_norm_fox[l], q_norm_mem[l],
              w_out[l], norm_ffn2[l], w_ffn2_gate[l], w_ffn2_up[l], w_ffn2_down[l], norm_final[l])
        mk_p, mv_p = _mem_kv(mem_prompt, norm_mem[l], w_mem_kv[l], k_norm_mem[l])
        zero_conv = jnp.zeros((bp, CONV_K - 1, CONV_DIM), yp.dtype)
        zero_kv = jnp.zeros((bp, 0, FOX_HEADS, HEAD_DIM), yp.dtype)
        zero_f = jnp.zeros((bp, 0, FOX_HEADS), F32)
        yp, k_p, v_p, f_p, c_p = _layer(yp, zero_conv, zero_kv, zero_kv, zero_f, mk_p, mv_p, lp)
        ys, k_s, v_s, f_s, c_s = _layer(ys, state_conv[l], cache_fox_k[l], cache_fox_v[l],
                                         cache_fox_logf[l], cache_mem_k[l], cache_mem_v[l], lp)
        kp_l.append(k_p); vp_l.append(v_p); fp_l.append(f_p); cp_l.append(c_p)
        mkp_l.append(mk_p); mvp_l.append(mv_p)
        ks_l.append(k_s); vs_l.append(v_s); fs_l.append(f_s); cs_l.append(c_s)
    return (yp, ys,
            jnp.stack(kp_l), jnp.stack(vp_l), jnp.stack(fp_l), jnp.stack(cp_l),
            jnp.stack(mkp_l), jnp.stack(mvp_l),
            jnp.stack(ks_l), jnp.stack(vs_l), jnp.stack(fs_l), jnp.stack(cs_l))


_drawn_inputs = setup_inputs


def setup_inputs(seed=0):
    import zlib

    import numpy as np

    out = dict(_drawn_inputs(seed))
    spreads = {}
    factors = {'cache_fox_logf': 33.176,
     'norm_ffn1': 4.687,
     'conv_b': 34.477,
     'q_norm_fox': 48.733,
     'k_norm_fox': 7.917,
     'q_norm_mem': 8.0,
     'k_norm_mem': 11.071,
     'norm_mem': 2.786,
     'norm_ffn2': 7.963,
     'norm_final': 8.569,
     'state_conv': 3.53}
    for name, (base, spread) in spreads.items():
        noise = np.random.default_rng([zlib.crc32(name.encode()), seed]).standard_normal(out[name].shape)
        drawn = base * np.exp(spread * noise) if base else spread * noise
        out[name] = __import__('jax').numpy.asarray(drawn.astype(out[name].dtype))
    for name, factor in factors.items():
        out[name] = (out[name] * factor).astype(out[name].dtype)
    return out
```

```python
import concourse.bass as bass
import concourse.mybir as mybir
from concourse.alu_op_type import AluOpType as ALU
from contextlib import ExitStack, nullcontext

F32 = mybir.dt.float32
F32R = mybir.dt.float32r
BF16 = mybir.dt.bfloat16
ACT = mybir.ActivationFunctionType
AX = mybir.AxisListType

P = 128
EPS = 1e-6
MASKED = -1e30

EXP_LN_SET = "natural_log_exp_and_others"
SILU_SET = "silu_and_others"


def hybrid_step(nc, i, o):
    D = i["x_prompt"].shape[2]
    SEQ = i["x_prompt"].shape[1]
    DEC = i["x_sample"].shape[1]
    PAST = i["cache_fox_k"].shape[2]
    NMEM = i["mem_prompt"].shape[1]
    DFF = i["w_ffn1_gate"].shape[2]
    HD = i["q_norm_fox"].shape[1]
    CONV = i["state_conv"].shape[3]
    FH = i["b_forget"].shape[1]
    FOX = FH * HD
    MEM = i["w_mem_kv"].shape[2] // 2
    T = SEQ + DEC
    KT = D // P
    PAIR = P // HD
    CHUNKS = [(0, 384), (384, 384), (768, T - 768)]
    CN = 384
    TILES = [(t * P, min(P, T - t * P)) for t in range((T + P - 1) // P)]
    NT = len(TILES)
    PT = SEQ // P
    NF = DFF // (2 * P)
    KEYS = SEQ + PAST + DEC
    U0, C0, B0 = 0, CONV, 2 * CONV
    Q0 = 3 * CONV
    K0, V0, FG0 = Q0 + FOX, Q0 + 2 * FOX, Q0 + 3 * FOX
    QM0 = FG0 + FH
    SCALE = float(HD) ** -0.5

    ctx = ExitStack()
    with ctx:
        def sb(name, shape, dt=F32, scope=ctx):
            return scope.enter_context(nc.sbuf_tensor(name, shape, dt))

        def sem(name):
            return ctx.enter_context(nc.semaphore(name))

        PS = ctx.enter_context(nc.psum_tensor("banks", [P, 8 * 512], F32))

        def bank(b, n, rows=P):
            return PS[0:rows, 512 * b:512 * b + n]

        xT = sb("xT", [P, KT, T])
        hh = sb("h_hi", [P, KT, T], F32R)
        hl = sb("h_lo", [P, KT, T], F32R)
        raw = sb("w_raw", [P, 4, KT * P])
        whi = sb("w_hi", [P, 4, KT * P], F32R)
        wlo = sb("w_lo", [P, 4, KT * P], F32R)
        ident = sb("ident", [P, P])
        onesD = sb("ones_over_d", [P, P])
        onesH = sb("ones_over_head", [P, P])
        identb = sb("ident_bf", [P, P], BF16)
        maskb = sb("mask_bf", [P, P], BF16)
        epsc = sb("eps", [P, 1])
        onec = sb("one", [P, 1])
        gain = sb("gains", [P, 4, KT])
        hgain = sb("head_gains", [P, 6])
        cvw = sb("conv_weights", [P, 4, CONV // P])
        bfor = sb("b_forget_col", [FH, 1])
        Ftok = sb("F_by_token", [P, NT, FH])
        ltok = sb("logf_by_token", [P, NT, FH])
        tiny = sb("tiny", [P, 16])

        x0s = ExitStack()
        xtok = sb("x_by_token", [P, NT, D], F32, x0s)
        x0s.close()
        fs = ExitStack()
        rawd = sb("wd_raw", [P, 2, D], F32, fs)
        whid = sb("wd_hi", [P, 2, D], F32R, fs)
        wlod = sb("wd_lo", [P, 2, D], F32R, fs)
        acth = sb("act_hi", [P, 2, T], F32R, fs)
        actl = sb("act_lo", [P, 2, T], F32R, fs)
        silu = sb("silu", [P, 2, CN], F32, fs)
        actf = sb("act_f32", [P, 2, CN], F32, fs)
        nsq = sb("norm_squares", [P, KT, CN], F32, fs)
        nsum = sb("norm_sum", [P, CN], F32, fs)
        nr0 = sb("norm_r0", [P, CN], F32, fs)
        nr = sb("norm_rstd", [P, CN], F32, fs)
        hf = sb("h_f32", [P, 4, CN], F32, fs)
        fs.close()
        ms_ = ExitStack()
        mixh = sb("mix_hi", [P, T], F32R, ms_)
        mixl = sb("mix_lo", [P, T], F32R, ms_)
        mixf = sb("mix_f32", [P, T], F32, ms_)
        qz = sb("qT_by_head", [P, PAIR, T], F32, ms_)
        qT = qz[:, 0, :]
        vT = sb("vT", [P, T], F32, ms_)
        hsq = sb("head_squares", [P, 2, CN], F32, ms_)
        hr0 = sb("head_r0", [P, 2, CN], F32, ms_)
        hr = sb("head_rstd", [P, CN], F32, ms_)
        cs = ExitStack()
        cin = sb("conv_in", [P, T + 4], F32, cs)
        cu, cacc = vT, qT
        wfr = sb("wf_raw", [P, KT, FH], F32, cs)
        wfh = sb("wf_hi", [P, KT, P], F32R, cs)
        wfl = sb("wf_lo", [P, KT, P], F32R, cs)
        fz = sb("f_z", [FH, T], F32, cs)
        fe = sb("f_e", [FH, T], F32, cs)
        fone = sb("f_ones", [FH, SEQ], F32, cs)
        FL = sb("logf_rows", [FH, KEYS], F32, cs)
        FC = sb("F_rows", [FH, KEYS], F32, cs)
        FN = sb("minusF_rows", [FH, KEYS], F32, cs)
        pastl = sb("past_logf", [P, FH], F32, cs)
        cs.close()
        xs = ExitStack()
        fx = dict(
            kT=sb("kT", [P, KEYS], F32, xs), ktok=sb("k_by_token", [P, NT, P], F32, xs),
            vtok=sb("v_by_token", [P, NT, P], F32, xs), ck=sb("past_k", [P, 1, P], F32, xs),
            cv=sb("past_v", [P, 1, P], F32, xs), prob=sb("probs", [P, 2, SEQ], F32, xs),
            pT=sb("probsT", [P, 2, SEQ], F32, xs), osb=sb("o_by_token", [P, 2, P], F32, xs),
            m=sb("row_max", [P, 20], F32, xs), b=sb("row_bias", [P, 20], F32, xs),
            s=sb("row_sum", [P, 20], F32, xs), r=sb("row_rsum", [P, 20], F32, xs))
        nF = sb("minusF", [P, PAIR, KEYS], F32, xs)
        Fp = sb("F_pair", [P, NT, PAIR], F32, xs)
        xs.close()
        es = ExitStack()
        mm_ = dict(
            kT=sb("mkT", [P, 2 * NMEM], F32, es), ktok=sb("mk_by_token", [P, 2, P], F32, es),
            vtok=sb("mv_by_token", [P, 2, P], F32, es), ck=sb("cache_mk", [P, 2, P], F32, es),
            cv=sb("cache_mv", [P, 2, P], F32, es), prob=sb("mprobs", [P, 2, NMEM], F32, es),
            pT=sb("mprobsT", [P, 2, NMEM], F32, es), osb=sb("mo_by_token", [P, 2, P], F32, es),
            m=sb("mrow_max", [P, 20], F32, es), b=sb("mrow_bias", [P, 20], F32, es),
            s=sb("mrow_sum", [P, 20], F32, es), r=sb("mrow_rsum", [P, 20], F32, es))
        memtok = sb("mem_by_token", [P, 2, D], F32, es)
        memsq = PS[:, 0:D]
        memf = [b[:, 0:4 * NMEM].rearrange("p (k n) -> p k n", k=4) for b in (mixf, vT)]
        memh = sb("memT_hi", [P, KT, NMEM], F32R, es)
        meml = sb("memT_lo", [P, KT, NMEM], F32R, es)
        es.close()
        ms_.close()

        negF_rows = nc.dram_tensor("negF_rows", (FH, KEYS), F32, kind="Internal").ap()

        s_const = sem("consts_made")
        s_small = sem("small_loads")
        s_smallc = sem("small_columns_ready")
        s_out = sem("outputs_stored")

        def semaphores(tag, names):
            return {n: sem(f"{tag}_{n}") for n in names.split()}

        x0 = semaphores("x0", "loaded0 loaded1 loaded2 turned copied_lo copied_hi")
        FFN = [semaphores(f"ffn{n}", "loaded_a loaded_b dloaded hi_a hi_b lo_a lo_b dhi dlo gate_done up_done silu_done "
                    "act_made act_hi act_lo down_done resid") for n in (1, 2)]
        NORM = [semaphores(f"norm{n}", "squares sums mean rough dve hi lo") for n in (1, 2, 3)]
        fg = semaphores("forget", "wloaded wsplit proj dve act past turned copied stored")
        LOOPS = {k: semaphores(k, "wloaded oloaded w_hi w_lo o_hi o_lo proj odone resid mix stored" + more)
                 for k, more in (("conv", " state_loaded act dve"), ("fox", " dve"), ("mem", ""))}
        ATT = {k: semaphores(k + "_att", "cloaded squares sums rough nrm vcopied tturned tcopied scores smax expd pturned "
                       "pcopied pv orow") for k in ("fox", "mem")}
        mp = semaphores("memprep", "loaded scaled act dve turned split")
        fin = semaphores("final", "turned dve act gain stored_a stored_b stored_c")
        row_stored = (fin["stored_a"], fin["stored_b"], fin["stored_c"])
        ITER = {"conv": CONV // P, "fox": FOX // P, "mem": MEM // P}
        ORDER = ["conv", "fox", "mem"]
        ROW0 = {"conv": 0, "fox": CONV, "mem": CONV + FOX}

        WG = [i["w_ffn1_gate"][0], i["w_ffn2_gate"][0]]
        WU = [i["w_ffn1_up"][0], i["w_ffn2_up"][0]]
        WD = [i["w_ffn1_down"][0], i["w_ffn2_down"][0]]
        w_in, w_out = i["w_in"][0], i["w_out"][0]
        w_kv = i["w_mem_kv"][0]
        xp, xsm = i["x_prompt"][0], i["x_sample"][0]

        def cols(w, start, n=P):
            return w.rearrange("(k p) n -> p k n", p=P)[:, :, bass.ds(start, n)]

        def repeated(eng, n):
            return nullcontext(0) if n == 1 else eng.Fori(0, n)

        wait_regs = {}

        def wait_apart(eng, sem_, value):
            if not isinstance(value, int):
                r = wait_regs.get(str(eng.engine)) or eng.alloc_register(f"wait_{eng.engine}")
                wait_regs[str(eng.engine)] = r
                eng.reg_add(r, value - 1, 1)
                value = r
            eng.wait_ge(s_const, 12)
            eng.wait_ge(sem_, value)

        def split3(eng, out, w_hi, w_lo, x_hi, x_lo, first, last):
            eng.matmul(out, w_hi, x_hi, start=first, stop=False)
            eng.matmul(out, w_hi, x_lo, start=False, stop=False)
            return eng.matmul(out, w_lo, x_hi, start=False, stop=last)

        block = ctx.enter_context(nc.Block())

        NA = 2 * NT
        UNITS = [(a // 2, a % 2) for a in range(NA)]
        FOXU = [(t, j, TILES[t][1], (t + 1) * P if t < PT else PAST + DEC) for t, j in UNITS]
        MEMU = [(t, j, TILES[t][1], NMEM) for t, j in UNITS]
        KIND = {"fox": FOXU, "mem": MEMU}

        def kblocks(kind, a):
            W = KIND[kind][a][3]
            return [(c, min(P, W - c)) for c in range(0, W, P)]

        def groups(kind, a):
            k = kblocks(kind, a)
            return [k[g:g + 4] for g in range(0, len(k), 4)]

        def turn_order(kind):
            seq = [("p", 0, g) for g in range(len(groups(kind, 0)))]
            for a in range(NA):
                if a + 1 < NA:
                    seq += [("p", a + 1, g) for g in range(len(groups(kind, a + 1)))]
                if a % 2 == 0 and a >= 2:
                    seq.append(("o", a // 2 - 1, 0))
            seq.append(("o", NT - 1, 0))
            return {x: n for n, x in enumerate(seq)}
        TURN = {k: turn_order(k) for k in ("fox", "mem")}
        NTURN = {k: len(TURN[k]) for k in TURN}

        PROJ = {"fox": [("k", 0, c) for c in range(3)] + [("q", 1, c) for c in range(3)] +
                       [("v", 2, c) for c in range(3)],
                "mem": [("q", 0, c) for c in range(3)] + [("k", 1, 0), ("v", 2, 0)]}
        PBANK = {"fox": [0, 1, 2, 3, 4, 5, 0, 1, 2], "mem": [0, 1, 2, 3, 4]}
        NORMED = {k: [n for n, u in enumerate(PROJ[k]) if u[0] != "v"] for k in PROJ}
        NV = {k: sum(u[0] == "v" for u in PROJ[k]) for k in PROJ}

        def span(kind, n):
            what, _, c = PROJ[kind][n]
            return (0, NMEM) if kind == "mem" and what != "q" else CHUNKS[c]

        def pieces(kind, n):
            what, _, c = PROJ[kind][n]
            s, w = span(kind, n)
            if what == "q":
                return [("q0", s, 0, w), ("q1", s, 0, w)]
            if kind == "mem" or s + w <= SEQ:
                return [("k", s, 0, w)]
            return [("k", s, 0, SEQ - s), ("k", SEQ + PAST, SEQ - s, DEC)]

        def nrm_count(kind, m):
            return sum(3 + len(pieces(kind, n)) for n in NORMED[kind][:m + 1])
        NRM = {k: nrm_count(k, len(NORMED[k]) - 1) for k in PROJ}

        TT = {"fox": [("k", 0, 4), ("k", 4, 4), ("k", 8, 1), ("c", 0, 1), ("v", 0, 4), ("v", 4, 4), ("v", 8, 1)],
              "mem": [("k", 0, 2), ("c", 0, 2), ("v", 0, 2)]}
        NTT = {k: len(TT[k]) for k in TT}
        TTV = {k: [n for n, g in enumerate(TT[k]) if g[0] == "v"] for k in TT}

        def tile_rows(kind, t):
            return TILES[t][1] if kind == "fox" else P

        def tok_source(kind, what, t):
            n = tile_rows(kind, t)
            if what == "v":
                return vT[:, t * P:t * P + n]
            kT = (fx if kind == "fox" else mm_)["kT"]
            at = t * P if kind == "mem" or t < PT else SEQ + PAST
            return kT[:, at:at + n]

        BUF = {"fox": fx, "mem": mm_}

        CPIECES = [(0, 384, 0, 0), (384, 384, 0, 1), (768, SEQ - 768, 0, 2), (SEQ, DEC, 2, 2)]
        CBANK = [3, 4, 5, 6, 7, 0, 1, 2, 3]
        MBANK = [4, 0, 4]
        OBANK = {"conv": 4, "fox": 0, "mem": 0}

        def rsum_step(a):
            return 2 * a if a else 1

        def ocopy_step(a):
            return 2 * a + 3 if a < NA - 1 else 2 * NA

        @block.sync
        def _(sp):
            def load_x(c):
                for t in range(3 * c, 3 * c + 3):
                    s, n = TILES[t]
                    src = xp[s:s + n, :] if t < PT else xsm[:, :]
                    sp.dma_start(xtok[0:n, t, :], src).then_inc(x0[f"loaded{c}"], 16)
            load_x(0)
            load_x(1)
            with nc.allow_non_contiguous_dma(reason="small columns"):
                for n, name in enumerate(("norm_ffn1", "norm_mix", "norm_ffn2", "norm_mem")):
                    sp.dma_start(gain[:, n, :], i[name][0].rearrange("(k p) -> p k", p=P)).then_inc(s_small, 16)
                for n, name in enumerate(("q_norm_fox", "k_norm_fox", "q_norm_mem", "k_norm_mem")):
                    for h in range(PAIR):
                        sp.dma_start(hgain[h * HD:(h + 1) * HD, n:n + 1],
                                     i[name][0].rearrange("(p a) -> p a", a=1)).then_inc(s_small, 16)
                for n in range(3):
                    sp.dma_start(cvw[:, n, :], i["conv_w"][0, n].rearrange("(k p) -> p k", p=P)).then_inc(s_small, 16)
                sp.dma_start(cvw[:, 3, :], i["conv_b"][0].rearrange("(k p) -> p k", p=P)).then_inc(s_small, 16)
                sp.dma_start(bfor[:, :], i["b_forget"][0].rearrange("(p a) -> p a", a=1)).then_inc(s_small, 16)

            def load_gu(n, g, j):
                f = FFN[n]
                for half, w in enumerate((WG[n], WU[n])):
                    sp.dma_start(raw[:, 2 * j + half, :].rearrange("p (k n) -> p k n", k=KT),
                                 cols(w, g * 2 * P + j * P)).then_inc((f["loaded_a"], f["loaded_b"])[j], 16)

            def load_down(n, g):
                for j in range(2):
                    sp.dma_start(rawd[:, j, :], WD[n][bass.ds(g * 2 * P + j * P, P), :]).then_inc(FFN[n]["dloaded"], 16)

            def ffn_loads(n):
                f = FFN[n]
                load_down(n, 0)
                with repeated(sp, NF - 1) as g:
                    for j in range(2):
                        sp.wait_ge((f["lo_a"], f["lo_b"])[j], g + 1)
                        load_gu(n, g + 1, j)
                    sp.wait_ge(f["dlo"], g + 1)
                    load_down(n, g + 1)

            load_gu(0, 0, 0)
            load_x(2)
            load_gu(0, 0, 1)
            sp.wait_ge(x0["turned"], 2 * NT)
            ffn_loads(0)

            def load_mixer(kind, it):
                L = LOOPS[kind]
                src = {"conv": [(w_in, U0), (w_in, C0), (w_in, B0)], "fox": [(w_in, K0), (w_in, Q0), (w_in, V0)],
                       "mem": [(w_in, QM0), (w_kv, 0), (w_kv, MEM)]}[kind]
                for b, (w, c) in enumerate(src):
                    sp.dma_start(raw[:, b, :].rearrange("p (k n) -> p k n", k=KT), cols(w, it * P + c))\
                      .then_inc(L["wloaded"], 16)

            def load_out(kind, it):
                sp.dma_start(raw[:, 3, :], w_out[bass.ds(it * P + ROW0[kind], P), :]).then_inc(LOOPS[kind]["oloaded"], 16)

            sp.wait_ge(FFN[0]["lo_a"], NF)
            sp.wait_ge(FFN[0]["lo_b"], NF)
            load_mixer("conv", 0)
            load_out("conv", 0)
            sp.wait_ge(NORM[1]["lo"], 3 * KT)
            with nc.allow_non_contiguous_dma(reason="8 columns"):
                sp.dma_start(wfr[:, :, :], cols(w_in, FG0, FH)).then_inc(fg["wloaded"], 16)
                sp.dma_start(pastl[:, :], i["cache_fox_logf"][0, 0]).then_inc(fg["wloaded"], 16)

            def step_ahead(kind, it):
                L = LOOPS[kind]
                sp.wait_ge(L["w_lo"], 3 * it + 3)
                load_mixer(kind, it + 1)

            def out_ahead(kind, it):
                sp.wait_ge(LOOPS[kind]["o_lo"], it + 1)
                load_out(kind, it + 1)

            def next_loop(kind):
                prev = ORDER[ORDER.index(kind) - 1]
                n = ITER[prev]
                sp.wait_ge(LOOPS[prev]["w_lo"], 3 * n)
                load_mixer(kind, 0)
                sp.wait_ge(LOOPS[prev]["o_lo"], n)
                load_out(kind, 0)

            L = LOOPS["conv"]
            state = i["state_conv"][0, 0].rearrange("s c -> c s")
            for it in range(ITER["conv"]):
                if it:
                    sp.wait_ge(L["stored"], 32 * it)
                    sp.wait_ge(L["mix"], 4 * it)
                with nc.allow_non_contiguous_dma(reason="conv state"):
                    sp.dma_start(cin[:, SEQ + 2:SEQ + 4], state[it * P:(it + 1) * P, :]).then_inc(L["state_loaded"], 16)
                if it + 1 < ITER["conv"]:
                    step_ahead("conv", it)
                else:
                    sp.wait_ge(L["w_lo"], 3 * ITER["conv"])
                    load_mixer("fox", 0)
                sp.wait_ge(L["dve"], 16 * it + 16)
                for name, c in (("conv_state_prompt", SEQ), ("conv_state_sample", T + 2)):
                    with nc.allow_non_contiguous_dma(reason="conv state"):
                        sp.dma_start(o[name][0, 0].rearrange("s c -> c s")[it * P:(it + 1) * P, :],
                                     cin[:, c:c + 2]).then_inc(L["stored"], 16)
                if it + 1 < ITER["conv"]:
                    out_ahead("conv", it)
                else:
                    sp.wait_ge(L["o_lo"], ITER["conv"])
                    load_out("fox", 0)

            sp.wait_ge(fg["dve"], 10)
            sp.dma_start(negF_rows, FN[:, :]).then_inc(fg["stored"], 16)
            sp.wait_ge(fg["copied"], 4)
            with nc.allow_non_contiguous_dma(reason="8 columns"):
                sp.dma_start(o["fox_logf_prompt"][0, 0].rearrange("(t p) h -> p t h", p=P), ltok[:, 0:PT, :])\
                  .then_inc(fg["stored"], 16)
                sp.dma_start(o["fox_logf_sample"][0, 0], ltok[0:DEC, PT, :]).then_inc(fg["stored"], 16)
            sp.wait_ge(fg["stored"], 48)
            sp.wait_ge(LOOPS["conv"]["resid"], 24 * ITER["conv"] + 4)

            def attention_io(kind, it, more):
                L, A, B = LOOPS[kind], ATT[kind], BUF[kind]
                n = 2 if kind == "mem" else 1
                sp.wait_ge(L["resid"], 24 * it + 4)
                if kind == "fox":
                    for j in range(PAIR):
                        sp.dma_start(nF[:, j, :], negF_rows[bass.ds(it * PAIR + j, 1), :].broadcast_to((P, KEYS)))\
                          .then_inc(A["cloaded"], 16)
                ck, cv = ("cache_fox_k", "cache_fox_v") if kind == "fox" else ("cache_mem_k", "cache_mem_v")
                for name, buf in ((ck, B["ck"]), (cv, B["cv"])):
                    src = i[name][0, 0].rearrange("(t p) h d -> p t (h d)", p=P)
                    sp.dma_start(buf[:, :, :], src[:, :, bass.ds(it * P, P)]).then_inc(A["cloaded"], 16)
                if more:
                    step_ahead(kind, it)
                for what, buf in (("k", B["ktok"]), ("v", B["vtok"])):
                    last = max(q for q, g in enumerate(TT[kind]) if g[0] == what)
                    sp.wait_ge(A["tcopied"], it * NTT[kind] + last + 1)
                    name = f"{kind}_{what}_prompt"
                    nt = PT if kind == "fox" else 2
                    dst = o[name][0, 0].rearrange("(t p) h d -> p t (h d)", p=P)
                    sp.dma_start(dst[:, :, bass.ds(it * P, P)], buf[:, 0:nt, :]).then_inc(L["stored"], 16)
                    if kind == "fox":
                        dst = o[f"fox_{what}_sample"][0, 0].rearrange("p h d -> p (h d)")
                        sp.dma_start(dst[:, bass.ds(it * P, P)], buf[0:DEC, PT, :]).then_inc(L["stored"], 16)
                wait_apart(sp, L["stored"], (64 if kind == "fox" else 32) * (it + 1))
                if more:
                    out_ahead(kind, it)

            with repeated(sp, ITER["fox"] - 1) as it:
                attention_io("fox", it, True)
            attention_io("fox", ITER["fox"] - 1, False)
            next_loop("mem")
            sp.wait_ge(LOOPS["fox"]["resid"], 24 * ITER["fox"] + 4)
            sp.dma_start(memtok[:, :, :], i["mem_prompt"][0].rearrange("(t p) d -> p t d", p=P)).then_inc(mp["loaded"], 16)
            with repeated(sp, ITER["mem"] - 1) as it:
                attention_io("mem", it, True)
            attention_io("mem", ITER["mem"] - 1, False)

            sp.wait_ge(LOOPS["mem"]["w_lo"], 3 * ITER["mem"])
            sp.wait_ge(LOOPS["mem"]["o_lo"], ITER["mem"])
            load_gu(1, 0, 0)
            load_gu(1, 0, 1)
            sp.wait_ge(LOOPS["mem"]["resid"], 24 * ITER["mem"] + 4)
            ffn_loads(1)

            sp.wait_ge(FFN[1]["lo_a"], NF)
            sp.wait_ge(FFN[1]["lo_b"], NF)
            sp.dma_start(raw[:, 3, :], i["norm_final"].broadcast_to((P, D))).then_inc(fin["gain"], 16)
            for t in range(NT):
                s, n = TILES[t]
                sp.wait_ge(fin["dve"], 6 * t + 6)
                dst = o["y_prompt"][0][s:s + n, :] if t < PT else o["y_sample"][0]
                sp.dma_start(dst, raw[0:n, t % 3, :]).then_inc(row_stored[t % 3], 16)
            for n, done in enumerate(row_stored):
                sp.wait_ge(done, 16 * len(range(n, NT, 3)))
            sp.wait_ge(LOOPS["conv"]["stored"], 32 * ITER["conv"])
            sp.wait_ge(fg["stored"], 48)

        @block.gpsimd
        def _(pool):
            pool.memset(ident[:, :], 0.0).then_inc(s_const, 1)
            pool.memset(identb[:, :], 0.0).then_inc(s_const, 1)
            pool.memset(maskb[:, :], 0.0).then_inc(s_const, 1)
            pool.memset(onesH[:, :], 0.0).then_inc(s_const, 1)
            pool.memset(onesD[:, :], 1.0 / D).then_inc(s_const, 1)
            pool.memset(epsc[:, :], EPS).then_inc(s_const, 1)
            pool.memset(onec[:, :], 1.0).then_inc(s_const, 1)
            pool.wait_ge(s_const, 7)
            for h in range(PAIR):
                pool.memset(onesH[h * HD:(h + 1) * HD, h * HD:(h + 1) * HD], 1.0 / HD).then_inc(s_const, 1)
            pool.wait_ge(s_const, 7 + PAIR)
            for m in (ident, identb):
                pool.affine_select(out=m[:, :], in_=m[:, :], compare_op=ALU.not_equal, fill=1.0, base=0,
                                   pattern=[[-1, P]], channel_multiplier=1).then_inc(s_const, 1)
            pool.affine_select(out=maskb[:, :], in_=maskb[:, :], compare_op=ALU.is_ge, fill=MASKED, base=0,
                               pattern=[[-1, P]], channel_multiplier=1).then_inc(s_const, 1)

            def norm_sums(n, c):
                N, w = NORM[n], CHUNKS[c][1]
                pool.wait_ge(N["squares"], c + 1)
                for st, half in enumerate((4, 2)):
                    if st:
                        pool.wait_ge(N["sums"], 3 * c + st)
                    pool.tensor_tensor(nsq[:, 0:half, 0:w], nsq[:, 0:half, 0:w], nsq[:, half:2 * half, 0:w],
                                       ALU.add).then_inc(N["sums"], 1)
                pool.wait_ge(N["sums"], 3 * c + 2)
                if c:
                    pool.wait_ge(N["mean"], c)
                pool.tensor_tensor(nsum[:, 0:w], nsq[:, 0, 0:w], nsq[:, 1, 0:w], ALU.add).then_inc(N["sums"], 1)

            def gu_lo(n, g, j):
                f = FFN[n]
                pool.wait_ge((f["hi_a"], f["hi_b"])[j], g + 1)
                pool.tensor_tensor(wlo[:, 2 * j:2 * j + 2, :], raw[:, 2 * j:2 * j + 2, :],
                                   whi[:, 2 * j:2 * j + 2, :].bitcast(F32), ALU.subtract)\
                    .then_inc((f["lo_a"], f["lo_b"])[j], 1)

            def ffn_group(n, g, more):
                f = FFN[n]
                pool.wait_ge(f["dhi"], g + 1)
                pool.tensor_tensor(wlod[:, :, :], rawd[:, :, :], whid[:, :, :].bitcast(F32), ALU.subtract)\
                    .then_inc(f["dlo"], 1)
                for u in range(6):
                    j, c = divmod(u, 3)
                    s, w = CHUNKS[c]
                    pool.wait_ge(f["act_hi"], 6 * g + u + 1)
                    pool.tensor_tensor(actl[:, j, s:s + w], actf[:, u % 2, 0:w], acth[:, j, s:s + w].bitcast(F32),
                                       ALU.subtract).then_inc(f["act_lo"], 1)
                    if more and c == 2:
                        gu_lo(n, g + 1, j)

            def ffn(n):
                with repeated(pool, NF - 1) as g:
                    ffn_group(n, g, True)
                ffn_group(n, NF - 1, False)

            norm_sums(0, 0)
            gu_lo(0, 0, 0)
            norm_sums(0, 1)
            gu_lo(0, 0, 1)
            ffn(0)

            def w_lo(L, it, b):
                pool.tensor_tensor(wlo[:, b, :], raw[:, b, :], whi[:, b, :].bitcast(F32), ALU.subtract)\
                    .then_inc(L["w_lo"], 1)

            def o_lo(L):
                pool.tensor_tensor(wlo[:, 3, :], raw[:, 3, :], whi[:, 3, :].bitcast(F32), ALU.subtract)\
                    .then_inc(L["o_lo"], 1)

            def conv_lo(it):
                L = LOOPS["conv"]
                for b in range(3):
                    pool.wait_ge(L["w_hi"], 3 * it + b + 1)
                    w_lo(L, it, b)
                pool.wait_ge(L["o_hi"], it + 1)
                o_lo(L)

            def split_in(kind, it, before):
                L = LOOPS[kind]
                before()
                wait_apart(pool, L["wloaded"], 48 * it + 48)
                for b in range(3):
                    pool.tensor_copy(whi[:, b, :], raw[:, b, :]).then_inc(L["w_hi"], 1)
                    pool.wait_ge(L["w_hi"], 3 * it + b + 1)
                    w_lo(L, it, b)

            def split_out(kind, it, before):
                L = LOOPS[kind]
                before()
                wait_apart(pool, L["oloaded"], 16 * it + 16)
                pool.tensor_copy(whi[:, 3, :], raw[:, 3, :]).then_inc(L["o_hi"], 1)
                pool.wait_ge(L["o_hi"], it + 1)
                o_lo(L)

            conv_lo(0)
            for c in range(2):
                norm_sums(1, c)
            pool.wait_ge(NORM[1]["lo"], 3 * KT)
            pool.memset(wfh[:, :, :].bitcast(F32), 0.0).then_inc(fg["wsplit"], 1)
            pool.memset(wfl[:, :, :].bitcast(F32), 0.0).then_inc(fg["wsplit"], 1)
            pool.memset(fone[:, :], 1.0).then_inc(fg["wsplit"], 1)
            pool.memset(cin[:, 0:2], 0.0).then_inc(fg["wsplit"], 1)
            pool.wait_ge(fg["wsplit"], 4)
            pool.wait_ge(fg["wloaded"], 32)
            pool.tensor_copy(wfh[:, :, 0:FH], wfr[:, :, :]).then_inc(fg["wsplit"], 1)
            pool.wait_ge(fg["wsplit"], 5)
            pool.tensor_tensor(wfl[:, :, 0:FH], wfr[:, :, :], wfh[:, :, 0:FH].bitcast(F32), ALU.subtract)\
                .then_inc(fg["wsplit"], 1)

            def used(kind, it):
                n = 9 if kind == "conv" else len(PROJ[kind])
                return lambda: pool.wait_ge(LOOPS[kind]["proj"], n * it + n)

            def out_used(kind, it):
                return lambda: pool.wait_ge(LOOPS[kind]["odone"], 24 * it + 24)

            def mix_split_conv(it):
                L = LOOPS["conv"]
                for p in range(4):
                    s, w = CPIECES[p][0:2]
                    pool.wait_ge(L["act"], 12 * it + 3 * p + 3)
                    pool.tensor_tensor(mixl[:, s:s + w], mixf[:, s:s + w], mixh[:, s:s + w].bitcast(F32),
                                       ALU.subtract).then_inc(L["mix"], 1)

            def mix_split(kind, it):
                L = LOOPS[kind]
                for t in range(NT):
                    s, w = TILES[t]
                    wait_apart(pool, ATT[kind]["pcopied"], NTURN[kind] * it + TURN[kind]["o", t, 0] + 1)
                    pool.tensor_copy(mixh[:, s:s + w], mixf[:, s:s + w]).then_inc(L["mix"], 1)
                    pool.wait_ge(L["mix"], 2 * NT * it + 2 * t + 1)
                    pool.tensor_tensor(mixl[:, s:s + w], mixf[:, s:s + w], mixh[:, s:s + w].bitcast(F32),
                                       ALU.subtract).then_inc(L["mix"], 1)

            for it in range(ITER["conv"]):
                last = it + 1 == ITER["conv"]
                mix_split_conv(it)
                if last:
                    split_in("fox", 0, used("conv", it))
                    split_out("fox", 0, out_used("conv", it))
                else:
                    conv_lo(it + 1)
            with repeated(pool, ITER["fox"] - 1) as it:
                split_in("fox", it + 1, used("fox", it))
                mix_split("fox", it)
                split_out("fox", it + 1, out_used("fox", it))
            split_in("mem", 0, used("fox", ITER["fox"] - 1))
            mix_split("fox", ITER["fox"] - 1)
            split_out("mem", 0, out_used("fox", ITER["fox"] - 1))
            for h in range(2):
                pool.wait_ge(mp["dve"], 5 + h)
                ks = slice(4 * h, 4 * h + 4)
                pool.tensor_copy(memh[:, ks, :], memf[h]).then_inc(mp["split"], 1)
                pool.wait_ge(mp["split"], 2 * h + 1)
                pool.tensor_tensor(meml[:, ks, :], memf[h], memh[:, ks, :].bitcast(F32), ALU.subtract)\
                    .then_inc(mp["split"], 1)
            with repeated(pool, ITER["mem"] - 1) as it:
                split_in("mem", it + 1, used("mem", it))
                mix_split("mem", it)
                split_out("mem", it + 1, out_used("mem", it))
            mix_split("mem", ITER["mem"] - 1)
            gu_lo(1, 0, 0)
            gu_lo(1, 0, 1)
            for c in range(2):
                norm_sums(2, c)
            ffn(1)

        @block.scalar
        def _(act):
            def x_copy(t):
                s, n = TILES[t]
                act.wait_ge(x0["turned"], 2 * t + 1)
                act.activation(xT[:, 0:4, s:s + n],
                               bank(2 * (t % 2), 512).rearrange("p (k n) -> p k n", k=4)[:, :, 0:n],
                               ACT.Copy).then_inc(x0["copied_lo"], 1)

            def norm_squares(n, c, ready):
                s, w = CHUNKS[c]
                ready(c)
                if c:
                    act.wait_ge(NORM[n]["sums"], 3 * c)
                act.activation(nsq[:, :, 0:w], xT[:, :, s:s + w], ACT.Square).then_inc(NORM[n]["squares"], 1)

            def rough(sem_, at, ms, r0):
                act.activation(r0, ms, ACT.Ln, bias=epsc[0:ms.shape[0], 0:1]).then_inc(sem_, 1)
                act.wait_ge(sem_, at + 1)
                act.activation(r0, r0, ACT.Exp, scale=-0.5).then_inc(sem_, 1)

            def norm_rest(n, c):
                N = NORM[n]
                s, w = CHUNKS[c]
                act.wait_ge(N["mean"], c + 1)
                if c:
                    act.wait_ge(N["dve"], 11 * c)
                rough(N["rough"], 2 * c, bank(MBANK[n] + c, w), nr0[:, 0:w])
                for k in range(KT):
                    act.wait_ge(N["dve"], 11 * c + 3 + k + 1)
                    act.activation(hh[:, k, s:s + w], hf[:, k % 4, 0:w], ACT.Copy).then_inc(N["hi"], 1)

            def norm(n, ready):
                norm_squares(n, 0, ready)
                norm_squares(n, 1, ready)
                norm_rest(n, 0)
                norm_squares(n, 2, ready)
                norm_rest(n, 1)
                norm_rest(n, 2)

            def gu_hi(n, g, j):
                f = FFN[n]
                act.wait_ge((f["loaded_a"], f["loaded_b"])[j], 32 * g + 32)
                act.activation(whi[:, 2 * j:2 * j + 2, :], raw[:, 2 * j:2 * j + 2, :], ACT.Copy)\
                    .then_inc((f["hi_a"], f["hi_b"])[j], 1)

            def ffn_group(n, g, more):
                f = FFN[n]
                act.wait_ge(f["dloaded"], 32 * g + 32)
                act.wait_ge(f["resid"], 24 * g + 4)
                act.activation(whid[:, :, :], rawd[:, :, :], ACT.Copy).then_inc(f["dhi"], 1)
                for u in range(6):
                    j, c = divmod(u, 3)
                    s, w = CHUNKS[c]
                    act.wait_ge(f["gate_done"], 6 * g + u + 1)
                    act.activation(silu[:, u % 2, 0:w], bank(2 * (u % 2), w), ACT.Silu).then_inc(f["silu_done"], 1)
                    act.wait_ge(f["act_made"], 6 * g + u + 3)
                    act.activation(acth[:, j, s:s + w], actf[:, u % 2, 0:w], ACT.Copy).then_inc(f["act_hi"], 1)
                    if more and c == 2:
                        act.wait_ge(f["up_done"], 6 * g + u + 1)
                        gu_hi(n, g + 1, j)

            def ffn(n):
                nc.scalar.preload_act_table_set(SILU_SET)
                with repeated(act, NF - 1) as g:
                    ffn_group(n, g, True)
                ffn_group(n, NF - 1, False)

            nc.scalar.preload_act_table_set(EXP_LN_SET)
            act.wait_ge(s_const, 12)

            def x_ready(c):
                act.wait_ge(x0["copied_lo"], 3 * c + 3)
                act.wait_ge(x0["copied_hi"], 3 * c + 3)

            for t in range(3):
                x_copy(t)
            norm_squares(0, 0, x_ready)
            for t in range(3, 6):
                x_copy(t)
            gu_hi(0, 0, 0)
            norm_squares(0, 1, x_ready)
            for t in range(6, 9):
                x_copy(t)
            norm_rest(0, 0)
            gu_hi(0, 0, 1)
            norm_squares(0, 2, x_ready)
            norm_rest(0, 1)
            norm_rest(0, 2)
            ffn(0)
            nc.scalar.preload_act_table_set(EXP_LN_SET)

            def conv_hi(it):
                L = LOOPS["conv"]
                act.wait_ge(L["wloaded"], 48 * it + 48)
                for b in range(3):
                    act.activation(whi[:, b, :], raw[:, b, :], ACT.Copy).then_inc(L["w_hi"], 1)
                act.wait_ge(L["oloaded"], 16 * it + 16)
                if it:
                    act.wait_ge(L["odone"], 24 * it)
                act.activation(whi[:, 3, :], raw[:, 3, :], ACT.Copy).then_inc(L["o_hi"], 1)

            act.wait_ge(FFN[0]["up_done"], 6 * NF)
            conv_hi(0)
            norm(1, lambda c: act.wait_ge(FFN[0]["resid"], 24 * (NF - 1) + 8 * (c + 1) + 4))

            def conv_step(it):
                L = LOOPS["conv"]
                for p, (s, w, sh, c) in enumerate(CPIECES):
                    col = s - CHUNKS[c][0]
                    act.wait_ge(L["proj"], 9 * it + 3 * c + 1)
                    act.activation(cu[:, s:s + w], PS[:, 512 * CBANK[3 * c] + col:512 * CBANK[3 * c] + col + w],
                                   ACT.Copy).then_inc(L["act"], 1)
                    act.wait_ge(L["dve"], 16 * it + 4 * p + 1)
                    act.activation(cacc[:, s:s + w], cin[:, s + sh + 2:s + sh + 2 + w], ACT.Identity,
                                   bias=cvw[:, 3, it:it + 1], scale=cvw[:, 2, it:it + 1]).then_inc(L["act"], 1)
                    act.wait_ge(L["dve"], 16 * it + 4 * p + 4)
                    act.activation(mixh[:, s:s + w], mixf[:, s:s + w], ACT.Copy).then_inc(L["act"], 1)

            for it in range(ITER["conv"]):
                conv_step(it)
                if it + 1 < ITER["conv"]:
                    conv_hi(it + 1)
                if it == 0:
                    act.wait_ge(fg["dve"], 4)
                    act.activation(fe[:, :], fe[:, :], ACT.Exp, scale=-1.0).then_inc(fg["act"], 1)
                    act.wait_ge(fg["act"], 1)
                    act.activation(fe[:, :], fe[:, :], ACT.Ln, bias=onec[0:FH, 0:1]).then_inc(fg["act"], 1)

            def pair_step(kind, it):
                A, B, L = ATT[kind], BUF[kind], LOOPS[kind]
                NP, NM = len(PROJ[kind]), len(NORMED[kind])
                for n, (what, _, c) in enumerate(PROJ[kind]):
                    s, w = span(kind, n)
                    act.wait_ge(L["proj"], NP * it + n + 1)
                    if what == "v":
                        act.activation(vT[:, s:s + w], bank(PBANK[kind][n], w), ACT.Copy).then_inc(A["vcopied"], 1)
                    else:
                        m = NORMED[kind].index(n)
                        if m >= 2:
                            act.wait_ge(A["sums"], NM * it + m - 1)
                        act.activation(hsq[:, m % 2, 0:w], bank(PBANK[kind][n], w), ACT.Square)\
                            .then_inc(A["squares"], 1)
                    m = n - 1
                    if m in NORMED[kind]:
                        head_rough(kind, it, NORMED[kind].index(m))
                for q, (what, t0, nt) in enumerate(TT[kind]):
                    act.wait_ge(A["tturned"], NTT[kind] * it + q + 1)
                    n = tile_rows(kind, t0) if what != "c" else P
                    src = bank(6 + q % 2, nt * P, n)
                    if what == "c":
                        at = SEQ if kind == "fox" else NMEM
                        act.activation(B["kT"][:, at:at + nt * P], src, ACT.Copy).then_inc(A["tcopied"], 1)
                    else:
                        dst = B["ktok" if what == "k" else "vtok"]
                        act.activation(dst[0:n, t0:t0 + nt, :], src.rearrange("p (t n) -> p t n", t=nt), ACT.Copy)\
                            .then_inc(A["tcopied"], 1)

                def exps(a):
                    t, j, rows, W = KIND[kind][a]
                    act.wait_ge(A["smax"], 2 * NA * it + 2 * a + 2)
                    if kind == "fox":
                        src = B["prob"][0:rows, a % 2, 0:W]
                    else:
                        src = PS[0:rows, 1024 * (a % 2):1024 * (a % 2) + W]
                        if a >= 2:
                            act.wait_ge(A["pturned"], NTURN[kind] * it + TURN[kind]["p", a - 2, 0] + 1)
                    act.activation(B["prob"][0:rows, a % 2, 0:W], src, ACT.Exp, bias=B["b"][0:rows, a:a + 1],
                                   accum_out=B["s"][0:rows, a:a + 1]).then_inc(A["expd"], 1)

                def turned(key):
                    n = TURN[kind][key]
                    act.wait_ge(A["pturned"], NTURN[kind] * it + n + 1)
                    b = 512 * (4 + n % 2)
                    if key[0] == "o":
                        s, w = TILES[key[1]]
                        act.activation(mixf[:, s:s + w], PS[:, b:b + w], ACT.Copy).then_inc(A["pcopied"], 1)
                        return
                    a = key[1]
                    rows = KIND[kind][a][2]
                    g = groups(kind, a)[key[2]]
                    if a >= 2 and key[2] == 0:
                        act.wait_ge(A["pv"], NA * it + a - 1)
                    full = [k for k in g if k[1] == P]
                    part = [k for k in g if k[1] < P]
                    for ks in (full, part):
                        if not ks:
                            continue
                        kr, c0 = ks[0][1], ks[0][0]
                        off = b + (c0 - g[0][0])
                        last = act.activation(
                            B["pT"][0:kr, a % 2, c0:c0 + len(ks) * P].rearrange("p (k n) -> p k n", n=P)[:, :, 0:rows]
                            if c0 + len(ks) * P <= B["pT"].shape[2] else B["pT"][0:kr, a % 2, c0:c0 + rows],
                            PS[0:kr, off:off + len(ks) * P].rearrange("p (k n) -> p k n", n=P)[:, :, 0:rows],
                            ACT.Copy)
                    last.then_inc(A["pcopied"], 1)

                exps(0)
                for g in range(len(groups(kind, 0))):
                    turned(("p", 0, g))
                exps(1)
                for a in range(NA):
                    if a + 1 < NA:
                        for g in range(len(groups(kind, a + 1))):
                            turned(("p", a + 1, g))
                    if a + 2 < NA:
                        exps(a + 2)
                    if a % 2 == 0 and a >= 2:
                        turned(("o", a // 2 - 1, 0))
                turned(("o", NT - 1, 0))

            def head_rough(kind, it, m):
                A = ATT[kind]
                w = span(kind, NORMED[kind][m])[1]
                n = len(NORMED[kind]) * it + m
                act.wait_ge(A["sums"], n + 1)
                rough(A["rough"], 2 * n, bank(6 + m % 2, w), hr0[:, m % 2, 0:w])

            with repeated(act, ITER["fox"]) as it:
                pair_step("fox", it)

            act.wait_ge(mp["loaded"], 16)
            act.wait_ge(LOOPS["fox"]["resid"], 24 * ITER["fox"] + 4)
            for t in range(2):
                if t:
                    act.wait_ge(mp["act"], t)
                act.activation(memsq, memtok[:, t, :], ACT.Square, accum_out=tiny[:, t:t + 1])\
                    .then_inc(mp["act"], 1)
            act.wait_ge(mp["dve"], 1)
            rough(mp["act"], 2, tiny[:, 2:4], tiny[:, 14:16])

            with repeated(act, ITER["mem"]) as it:
                pair_step("mem", it)

            act.wait_ge(LOOPS["mem"]["proj"], len(PROJ["mem"]) * ITER["mem"])
            gu_hi(1, 0, 0)
            act.wait_ge(LOOPS["mem"]["odone"], 24 * ITER["mem"])
            gu_hi(1, 0, 1)
            norm(2, lambda c: act.wait_ge(LOOPS["mem"]["resid"], 24 * (ITER["mem"] - 1) + 8 * (c + 1) + 4))
            ffn(1)

            nc.scalar.preload_act_table_set(EXP_LN_SET)
            for t in range(NT):
                s, n = TILES[t]
                act.wait_ge(fin["turned"], 2 * t + 2)
                if t:
                    act.wait_ge(fin["act"], 4 * t)
                for h in range(2):
                    act.activation(hf[0:n].rearrange("p k n -> p (k n)")[:, 512 * h:512 * h + 512], bank(2 * (t % 2) + h, 512, n), ACT.Square,
                                   accum_out=tiny[0:n, 4 + h:5 + h]).then_inc(fin["act"], 1)
                act.wait_ge(fin["dve"], 6 * t + 1)
                rough(fin["act"], 4 * t + 2, tiny[0:n, 6:7], tiny[0:n, 7:8])

        @block.vector
        def _(dve):
            for f in FFN:
                dve.sem_inc(f["act_made"], 2)
                dve.sem_inc(f["resid"], 4)
            for L in LOOPS.values():
                dve.sem_inc(L["resid"], 4)

            def x_copy(t):
                s, n = TILES[t]
                dve.wait_ge(x0["turned"], 2 * t + 2)
                dve.tensor_copy(xT[:, 4:8, s:s + n],
                                bank(1 + 2 * (t % 2), 512).rearrange("p (k n) -> p k n", k=4)[:, :, 0:n])\
                   .then_inc(x0["copied_hi"], 1)

            def rstd(sem_, at, ms, r0, r):
                dve.scalar_tensor_tensor(r, ms, EPS, r0, ALU.add, ALU.mult).then_inc(sem_, 1)
                dve.wait_ge(sem_, at + 1)
                dve.scalar_tensor_tensor(r, r, -0.5, r0, ALU.mult, ALU.mult).then_inc(sem_, 1)
                dve.wait_ge(sem_, at + 2)
                dve.scalar_tensor_tensor(r, r, 1.5, r0, ALU.add, ALU.mult).then_inc(sem_, 1)
                dve.wait_ge(sem_, at + 3)

            def norm_chunk(n, c):
                N = NORM[n]
                s, w = CHUNKS[c]
                dve.wait_ge(N["rough"], 2 * c + 2)
                if c:
                    dve.wait_ge(N["dve"], 11 * c)
                rstd(N["dve"], 11 * c, bank(MBANK[n] + c, w), nr0[:, 0:w], nr[:, 0:w])
                def lo(k):
                    dve.wait_ge(N["hi"], KT * c + k + 1)
                    dve.tensor_tensor(hl[:, k, s:s + w], hf[:, k % 4, 0:w], hh[:, k, s:s + w].bitcast(F32),
                                      ALU.subtract).then_inc(N["lo"], 1)

                for k in range(KT):
                    if KT * c + k >= 4:
                        dve.wait_ge(N["lo"], KT * c + k - 3)
                    dve.scalar_tensor_tensor(hf[:, k % 4, 0:w], xT[:, k, s:s + w], gain[:, n, k:k + 1],
                                             nr[:, 0:w], ALU.mult, ALU.mult).then_inc(N["dve"], 1)
                    if k >= 2:
                        lo(k - 2)
                lo(KT - 2)
                lo(KT - 1)

            def ffn(n):
                f = FFN[n]
                with repeated(dve, NF) as g:
                    for u in range(6):
                        w = CHUNKS[u % 3][1]
                        dve.wait_ge(f["silu_done"], 6 * g + u + 1)
                        dve.wait_ge(f["up_done"], 6 * g + u + 1)
                        if u >= 2:
                            dve.wait_ge(f["act_lo"], 6 * g + u - 1)
                        dve.tensor_tensor(actf[:, u % 2, 0:w], silu[:, u % 2, 0:w], bank(2 * (u % 2) + 1, w),
                                          ALU.mult).then_inc(f["act_made"], 1)
                    for c, (s, w) in enumerate(CHUNKS):
                        for d in range(KT):
                            m = KT * c + d
                            dve.wait_ge(f["down_done"], 24 * g + m + 1)
                            dve.scalar_tensor_tensor(xT[:, d, s:s + w], bank(4 + m % 4, w), 0.5, xT[:, d, s:s + w],
                                                     ALU.mult, ALU.add).then_inc(f["resid"], 1)

            for t in range(NT):
                x_copy(t)
            dve.wait_ge(s_small, 16 * (4 + 4 * PAIR + 5))
            dve.tensor_scalar(hgain[:, 4:5], hgain[:, 0:1], SCALE, None, ALU.mult).then_inc(s_smallc, 1)
            dve.tensor_scalar(hgain[:, 5:6], hgain[:, 2:3], SCALE, None, ALU.mult).then_inc(s_smallc, 1)
            dve.wait_ge(s_smallc, 2)
            norm_chunk(0, 0)
            norm_chunk(0, 1)
            norm_chunk(0, 2)
            ffn(0)
            for c in range(3):
                norm_chunk(1, c)

            def conv_step(it):
                L = LOOPS["conv"]
                for p, (s, w, sh, c) in enumerate(CPIECES):
                    col = s - CHUNKS[c][0]
                    base = 16 * it + 4 * p

                    def proj(which):
                        b = 512 * CBANK[3 * c + which] + col
                        return PS[:, b:b + w]
                    dve.wait_ge(L["proj"], 9 * it + 3 * c + 3)
                    dve.wait_ge(L["act"], 12 * it + 3 * p + 1)
                    if p == 0 and it == 0:
                        dve.wait_ge(fg["wsplit"], 4)
                    if p == 0 and it:
                        dve.wait_ge(L["stored"], 32 * it)
                    if p == 3:
                        dve.wait_ge(L["state_loaded"], 16 * it + 16)
                    dve.tensor_tensor(cin[:, s + sh + 2:s + sh + 2 + w], cu[:, s:s + w], proj(1), ALU.mult)\
                       .then_inc(L["dve"], 1)
                    dve.wait_ge(L["act"], 12 * it + 3 * p + 2)
                    for tap in range(2):
                        dve.wait_ge(L["dve"], base + 1 + tap)
                        dve.scalar_tensor_tensor(cacc[:, s:s + w], cin[:, s + sh + tap:s + sh + tap + w],
                                                 cvw[:, tap, it:it + 1], cacc[:, s:s + w], ALU.mult, ALU.add)\
                           .then_inc(L["dve"], 1)
                    dve.wait_ge(L["dve"], base + 3)
                    dve.tensor_tensor(mixf[:, s:s + w], cacc[:, s:s + w], proj(2), ALU.mult).then_inc(L["dve"], 1)

            def resid(kind, it):
                L = LOOPS[kind]
                for m in range(24):
                    c, d = divmod(m, KT)
                    s, w = CHUNKS[c]
                    dve.wait_ge(L["odone"], 24 * it + m + 1)
                    dve.tensor_tensor(xT[:, d, s:s + w], xT[:, d, s:s + w], bank(OBANK[kind] + m % 4, w), ALU.add)\
                       .then_inc(L["resid"], 1)

            for it in range(ITER["conv"]):
                conv_step(it)
                if it == 1:
                    dve.wait_ge(fg["act"], 2)
                    for a, b, n in ((0, 0, SEQ), (SEQ + PAST, SEQ, DEC)):
                        dve.scalar_tensor_tensor(FL[:, a:a + n], fz[:, b:b + n], 0.0, fe[:, b:b + n],
                                                 ALU.min, ALU.subtract).then_inc(fg["dve"], 1)
                    dve.wait_ge(fg["dve"], 7)
                    for a, n in ((0, SEQ), (SEQ, PAST + DEC)):
                        dve.tensor_tensor_scan(FC[:, a:a + n], fone[:, 0:n], FL[:, a:a + n], 0.0, ALU.mult, ALU.add)\
                           .then_inc(fg["dve"], 1)
                resid("conv", it)
                if it == 0:
                    for c, (s, w) in enumerate(CHUNKS):
                        dve.wait_ge(fg["proj"], c + 1)
                        dve.tensor_scalar(fz[:, s:s + w], bank(c, w, FH), bfor[:, 0:1], None, ALU.add).then_inc(fg["dve"], 1)
                    dve.wait_ge(fg["dve"], 3)
                    dve.scalar_tensor_tensor(fe[:, :], fz[:, :], -1.0, fz[:, :], ALU.mult, ALU.max).then_inc(fg["dve"], 1)
                    dve.wait_ge(fg["past"], 1)
                    dve.tensor_copy(FL[:, SEQ:SEQ + PAST], bank(3, PAST, FH)).then_inc(fg["dve"], 1)
            dve.wait_ge(fg["dve"], 9)
            dve.tensor_scalar(FN[:, :], FC[:, :], -1.0, None, ALU.mult).then_inc(fg["dve"], 1)
            for n, (dst, b) in enumerate(((ltok, 0), (Ftok, 1))):
                dve.wait_ge(fg["turned"], n + 1)
                dve.tensor_copy(dst[:, 0:PT, :], bank(b, PT * FH).rearrange("p (t h) -> p t h", h=FH))\
                   .then_inc(fg["copied"], 1)
                dve.tensor_copy(dst[0:DEC, PT, :], PS[0:DEC, 512 * b + PT * FH:512 * b + NT * FH])\
                   .then_inc(fg["copied"], 1)

            def pair_step(kind, it):
                A, B, L = ATT[kind], BUF[kind], LOOPS[kind]
                NM = len(NORMED[kind])
                dst = {"q0": qz[:, 0, :], "q1": qz[:, 1, :], "k": B["kT"]}
                part = {"q0": slice(0, HD), "q1": slice(HD, P), "k": slice(0, P)}
                g = {"q": hgain[:, 4:5] if kind == "fox" else hgain[:, 5:6],
                     "k": hgain[:, 1:2] if kind == "fox" else hgain[:, 3:4]}
                for m, n in enumerate(NORMED[kind]):
                    w = span(kind, n)[1]
                    at = NRM[kind] * it + nrm_count(kind, m - 1)
                    dve.wait_ge(A["rough"], 2 * (NM * it + m) + 2)
                    if m:
                        dve.wait_ge(A["nrm"], at)
                    rstd(A["nrm"], at, bank(6 + m % 2, w), hr0[:, m % 2, 0:w], hr[:, 0:w])
                    for what, c0, b0, pn in pieces(kind, n):
                        b = 512 * PBANK[kind][n] + b0
                        r = part[what]
                        dve.scalar_tensor_tensor(dst[what][r, c0:c0 + pn], PS[r, b:b + pn], g[what[0]][r],
                                                 hr[r, b0:b0 + pn], ALU.mult, ALU.mult).then_inc(A["nrm"], 1)
                if kind == "fox":
                    dve.tensor_copy(Fp[:, 0:PT, :], Ftok[:, 0:PT, bass.ds(it * PAIR, PAIR)]).then_inc(L["dve"], 1)
                    dve.tensor_copy(Fp[0:DEC, PT, :], Ftok[0:DEC, PT, bass.ds(it * PAIR, PAIR)]).then_inc(L["dve"], 1)
                    dve.wait_ge(L["dve"], 2 * it + 2)
                    dve.wait_ge(A["cloaded"], 64 * it + 64)

                def smax(a):
                    t, j, rows, W = KIND[kind][a]
                    sc = PS[0:rows, 1024 * (a % 2):1024 * (a % 2) + W]
                    m, b = B["m"][0:rows, a:a + 1], B["b"][0:rows, a:a + 1]
                    wait_apart(dve, A["scores"], NA * it + a + 1)
                    if kind == "fox":
                        if a >= 2:
                            last = TURN[kind]["p", a - 2, len(groups(kind, a - 2)) - 1]
                            wait_apart(dve, A["pturned"], NTURN[kind] * it + last + 1)
                        k0 = 0 if t < PT else SEQ
                        dve.tensor_tensor_reduce(B["prob"][0:rows, a % 2, 0:W], sc, nF[0:rows, j, k0:k0 + W], 1.0,
                                                 -3e38, ALU.add, ALU.max, m).then_inc(A["smax"], 1)
                        dve.wait_ge(A["smax"], 2 * NA * it + 2 * a + 1)
                        F_t = Fp[0:rows, t, j:j + 1]
                        dve.scalar_tensor_tensor(b, m, F_t, F_t, ALU.add, ALU.subtract, reverse1=True)\
                           .then_inc(A["smax"], 1)
                    else:
                        dve.reduce_max(m, sc, axis=AX.X).then_inc(A["smax"], 1)
                        dve.wait_ge(A["smax"], 2 * NA * it + 2 * a + 1)
                        dve.tensor_scalar(b, m, -1.0, None, ALU.mult).then_inc(A["smax"], 1)

                def rsum(a):
                    rows = KIND[kind][a][2]
                    dve.wait_ge(A["expd"], NA * it + a + 1)
                    dve.reciprocal(B["r"][0:rows, a:a + 1], B["s"][0:rows, a:a + 1]).then_inc(A["orow"], 1)

                smax(0)
                smax(1)
                rsum(0)
                for a in range(NA):
                    if a + 2 < NA:
                        smax(a + 2)
                    if a + 1 < NA:
                        rsum(a + 1)
                    t, j, rows, W = KIND[kind][a]
                    dve.wait_ge(A["pv"], NA * it + a + 1)
                    dve.wait_ge(A["orow"], 2 * NA * it + rsum_step(a))
                    if t >= 2 and j == 0:
                        dve.wait_ge(A["pturned"], NTURN[kind] * it + TURN[kind]["o", t - 2, 0] + 1)
                    dve.tensor_scalar(B["osb"][0:rows, t % 2, HD * j:HD * (j + 1)], bank(6 + j, HD, rows),
                                      B["r"][0:rows, a:a + 1], None, ALU.mult).then_inc(A["orow"], 1)
                resid(kind, it)

            dve.wait_ge(LOOPS["conv"]["dve"], 16 * ITER["conv"])
            dve.memset(qz[HD:P, 0, :], 0.0).then_inc(s_smallc, 1)
            dve.memset(qz[0:HD, 1, :], 0.0).then_inc(s_smallc, 1)
            dve.wait_ge(fg["stored"], 48)
            with repeated(dve, ITER["fox"]) as it:
                pair_step("fox", it)

            dve.wait_ge(mp["act"], 2)
            dve.tensor_scalar(tiny[:, 2:4], tiny[:, 0:2], 1.0 / D, None, ALU.mult).then_inc(mp["dve"], 1)
            dve.wait_ge(mp["act"], 4)
            rstd(mp["dve"], 1, tiny[:, 2:4], tiny[:, 14:16], tiny[:, 12:14])
            for t in range(2):
                dve.tensor_scalar(memtok[:, t, :], memtok[:, t, :], tiny[:, 12 + t:13 + t], None, ALU.mult)\
                   .then_inc(mp["scaled"], 1)
            for k in range(KT):
                dve.wait_ge(mp["turned"], k + 1)
                ins = dve.tensor_scalar(memf[k // 4][:, k % 4, :], PS[:, 512 * k:512 * k + NMEM], gain[:, 3, k:k + 1], None,
                                        ALU.mult)
                if k in (3, 7):
                    ins.then_inc(mp["dve"], 1)

            with repeated(dve, ITER["mem"]) as it:
                pair_step("mem", it)
            for c in range(3):
                norm_chunk(2, c)
            ffn(1)

            dve.wait_ge(fin["gain"], 16)
            for t in range(NT):
                n = TILES[t][1]
                v = tiny[0:n, 6:7]
                at = 6 * t
                dve.wait_ge(fin["act"], 4 * t + 2)
                if t:
                    dve.wait_ge(fin["dve"], at)
                dve.scalar_tensor_tensor(v, tiny[0:n, 4:5], tiny[0:n, 5:6], onesD[0:n, 0:1], ALU.add, ALU.mult)\
                   .then_inc(fin["dve"], 1)
                dve.wait_ge(fin["act"], 4 * t + 4)
                dve.wait_ge(fin["dve"], at + 1)
                r = tiny[0:n, 10:11]
                rstd(fin["dve"], at + 1, v, tiny[0:n, 7:8], r)
                if t >= 3:
                    dve.wait_ge(row_stored[t % 3], 16 * (t // 3))
                for h in range(2):
                    dve.scalar_tensor_tensor(raw[0:n, t % 3, 512 * h:512 * h + 512], bank(2 * (t % 2) + h, 512, n),
                                             r, raw[0:n, 3, 512 * h:512 * h + 512], ALU.mult, ALU.mult)\
                       .then_inc(fin["dve"], 1)

        @block.tensor
        def _(pe):
            pe.wait_ge(s_const, 12)

            def x_turn(t):
                s, n = TILES[t]
                pe.wait_ge(x0[f"loaded{t // 3}"], 48)
                if t >= 2:
                    pe.wait_ge(x0["copied_lo"], t - 1)
                    pe.wait_ge(x0["copied_hi"], t - 1)
                for k in range(KT):
                    b = 512 * (2 * (t % 2) + k // 4) + P * (k % 4)
                    mm = pe.transpose(PS[:, b:b + n], xtok[0:n, t, k * P:(k + 1) * P], ident[0:n, 0:n])
                    if k % 4 == 3:
                        mm.then_inc(x0["turned"], 1)

            def norm_mean(n, c):
                w = CHUNKS[c][1]
                if c == 2:
                    pe.wait_ge(NORM[n]["squares"], c + 1)
                    for k in range(KT):
                        mm = pe.matmul(bank(MBANK[n] + c, w), onesD[:, :], nsq[:, k, 0:w], start=k == 0,
                                       stop=k == KT - 1)
                    mm.then_inc(NORM[n]["mean"], 1)
                    return
                pe.wait_ge(NORM[n]["sums"], 3 * c + 3)
                pe.matmul(bank(MBANK[n] + c, w), onesD[:, :], nsum[:, 0:w], start=True, stop=True).then_inc(NORM[n]["mean"], 1)

            def product(b, block, x_hi, x_lo, s, w, fresh=None):
                for k in range(KT):
                    if fresh:
                        n, c = fresh
                        pe.wait_ge(NORM[n]["lo"], KT * c + k + 1)
                    ks = slice(k * P, (k + 1) * P)
                    mm = split3(pe, bank(b, w), whi[:, block, ks], wlo[:, block, ks], x_hi[:, k, s:s + w],
                                x_lo[:, k, s:s + w], k == 0, k == KT - 1)
                return mm

            def ffn(n):
                f = FFN[n]
                m = 2 * n

                def group(g, first):
                    for u in range(6):
                        j, c = divmod(u, 3)
                        s, w = CHUNKS[c]
                        if c == 0:
                            pe.wait_ge((f["lo_a"], f["lo_b"])[j], g + 1)
                        pe.wait_ge(f["act_made"], 6 * g + u + 1)
                        product(2 * (u % 2), 2 * j, hh, hl, s, w, (m, c) if first and j == 0 else None)\
                            .then_inc(f["gate_done"], 1)
                        if first and u < 2:
                            norm_mean(m, c + 1)
                        product(2 * (u % 2) + 1, 2 * j + 1, hh, hl, s, w).then_inc(f["up_done"], 1)
                    pe.wait_ge(f["dlo"], g + 1)
                    for e in range(24):
                        c, d = divmod(e, KT)
                        s, w = CHUNKS[c]
                        if d == 0:
                            pe.wait_ge(f["act_lo"], 6 * g + 3 + c + 1)
                        pe.wait_ge(f["resid"], 24 * g + e + 1)
                        for j in range(2):
                            mm = split3(pe, bank(4 + e % 4, w), whid[:, j, d * P:(d + 1) * P],
                                        wlod[:, j, d * P:(d + 1) * P], acth[:, j, s:s + w], actl[:, j, s:s + w],
                                        j == 0, j == 1)
                        mm.then_inc(f["down_done"], 1)

                group(0, True)
                with pe.Fori(1, NF) as g:
                    group(g, False)

            for t in range(NT):
                x_turn(t)
            norm_mean(0, 0)
            pe.wait_ge(x0["copied_lo"], NT)
            pe.wait_ge(x0["copied_hi"], NT)
            ffn(0)
            pe.wait_ge(FFN[0]["act_made"], 6 * NF + 2)

            def forget_gates():
                pe.wait_ge(fg["wsplit"], 6)
                for c, (s, w) in enumerate(CHUNKS):
                    for k in range(KT):
                        mm = split3(pe, bank(c, w), wfh[:, k, :], wfl[:, k, :], hh[:, k, s:s + w],
                                    hl[:, k, s:s + w], k == 0, k == KT - 1)
                    mm.then_inc(fg["proj"], 1)
                pe.wait_ge(fg["wloaded"], 32)
                pe.transpose(bank(3, PAST, FH), pastl[:, :], ident[:, :]).then_inc(fg["past"], 1)

            def out_product(kind, it, count):
                L = LOOPS[kind]
                pe.wait_ge(L["o_lo"], it + 1)
                for m in range(24):
                    c, d = divmod(m, KT)
                    s, w = CHUNKS[c]
                    if d == 0:
                        wait_apart(pe, L["mix"], count[-1] * it + count[c])
                    pe.wait_ge(L["resid"], 24 * it + m + 1)
                    split3(pe, bank(OBANK[kind] + m % 4, w), whi[:, 3, d * P:(d + 1) * P], wlo[:, 3, d * P:(d + 1) * P],
                           mixh[:, s:s + w], mixl[:, s:s + w], True, True).then_inc(L["odone"], 1)

            L = LOOPS["conv"]
            for it in range(ITER["conv"]):
                for c, (s, w) in enumerate(CHUNKS):
                    if it == 0 and c == 0:
                        norm_mean(1, 0)
                    for b in range(3):
                        if it == 0 and b == 1 and c < 2:
                            norm_mean(1, c + 1)
                        q = 3 * c + b
                        if c == 0:
                            pe.wait_ge(L["w_lo"], 3 * it + b + 1)
                        if it and q == 1:
                            pe.wait_ge(L["resid"], 24 * it + 4)
                        if it == 0 and q == 1:
                            pe.wait_ge(FFN[0]["resid"], 24 * NF + 4)
                        if it == 0 and q in (5, 6):
                            pe.wait_ge(NORM[1]["dve"], 11 * (0, 2)[q - 5] + 3)
                        if it == 1 and q == 0:
                            pe.wait_ge(fg["dve"], 5)
                        if q == 8:
                            pe.wait_ge(L["act"], 12 * it + 1)
                        product(CBANK[q], b, hh, hl, s, w, (1, c) if it == 0 and b == 0 else None)\
                            .then_inc(L["proj"], 1)
                pe.wait_ge(L["dve"], 16 * it + 8)
                out_product("conv", it, (1, 2, 4))
                if it == 0:
                    forget_gates()
            pe.wait_ge(fg["dve"], 9)
            for n, (src, b) in enumerate(((FL, 0), (FC, 1))):
                for t, (s, w) in enumerate(TILES):
                    at = s if t < PT else SEQ + PAST
                    mm = pe.transpose(PS[0:w, 512 * b + t * FH:512 * b + (t + 1) * FH], src[:, at:at + w],
                                      ident[0:FH, 0:FH])
                mm.then_inc(fg["turned"], 1)
            pe.wait_ge(fg["copied"], 4)

            def pair_step(kind, it):
                A, B, L = ATT[kind], BUF[kind], LOOPS[kind]
                NP, NM = len(PROJ[kind]), len(NORMED[kind])
                x = {("mem", "k"): (memh, meml), ("mem", "v"): (memh, meml)}

                def head_sums(m):
                    w = span(kind, NORMED[kind][m])[1]
                    pe.wait_ge(A["squares"], NM * it + m + 1)
                    if m >= 2:
                        pe.wait_ge(A["nrm"], NRM[kind] * it + nrm_count(kind, m - 2))
                    pe.matmul(bank(6 + m % 2, w), onesH[:, :], hsq[:, m % 2, 0:w], start=True, stop=True)\
                      .then_inc(A["sums"], 1)

                pe.wait_ge(L["resid"], 24 * it + 4)
                for n, (what, b, c) in enumerate(PROJ[kind]):
                    s, w = span(kind, n)
                    pe.wait_ge(L["w_lo"], 3 * it + b + 1)
                    if PBANK[kind][n] in PBANK[kind][:n]:
                        m = NORMED[kind].index(PBANK[kind].index(PBANK[kind][n]))
                        pe.wait_ge(A["nrm"], NRM[kind] * it + nrm_count(kind, m))
                    xh, xl = x.get((kind, what), (hh, hl))
                    product(PBANK[kind][n], b, xh, xl, s, w).then_inc(L["proj"], 1)
                    if n - 1 in NORMED[kind]:
                        head_sums(NORMED[kind].index(n - 1))

                def turn_tokens(q):
                    what, t0, nt = TT[kind][q]
                    if q >= 2:
                        pe.wait_ge(A["tcopied"], NTT[kind] * it + q - 1)
                    for t in range(nt):
                        b = 512 * (6 + q % 2) + t * P
                        if what == "c":
                            mm = pe.transpose(PS[:, b:b + P], B["ck"][:, t, :], ident[:, :])
                        else:
                            n = tile_rows(kind, t0 + t)
                            mm = pe.transpose(PS[0:n, b:b + P], tok_source(kind, what, t0 + t), ident[:, :])
                    mm.then_inc(A["tturned"], 1)

                def scores(a):
                    t, j, rows, W = KIND[kind][a]
                    s = t * P
                    k0 = {("fox", True): 0, ("fox", False): SEQ, ("mem", True): 0, ("mem", False): NMEM}[kind, t < PT]
                    if a >= 2:
                        if kind == "fox":
                            wait_apart(pe, A["smax"], 2 * NA * it + 2 * (a - 2) + 1)
                        else:
                            wait_apart(pe, A["expd"], NA * it + a - 1)
                    base = 1024 * (a % 2)
                    for c in range(0, W, 512):
                        n = min(512, W - c)
                        diag = kind == "fox" and c + n == W
                        mm = pe.matmul(PS[0:rows, base + c:base + c + n], qz[:, j, s:s + rows],
                                       B["kT"][:, k0 + c:k0 + c + n], start=True, stop=not diag)
                        if diag:
                            mm = pe.matmul(PS[0:rows, base + W - rows:base + W], identb[0:rows, 0:rows],
                                           maskb[0:rows, 0:rows], start=False, stop=True)
                    mm.then_inc(A["scores"], 1)

                def free_turn_bank(n):
                    if n >= 2:
                        wait_apart(pe, A["pcopied"], NTURN[kind] * it + n - 1)

                def turn_probs(a):
                    rows = KIND[kind][a][2]
                    pe.wait_ge(A["expd"], NA * it + a + 1)
                    for gi, g in enumerate(groups(kind, a)):
                        n = TURN[kind]["p", a, gi]
                        free_turn_bank(n)
                        for e, (c, kr) in enumerate(g):
                            b = 512 * (4 + n % 2) + e * P
                            mm = pe.transpose(PS[0:kr, b:b + rows], B["prob"][0:rows, a % 2, c:c + kr],
                                              ident[0:rows, 0:rows])
                        mm.then_inc(A["pturned"], 1)

                def weigh(a):
                    t, j, rows, W = KIND[kind][a]
                    last = TURN[kind]["p", a, len(groups(kind, a)) - 1]
                    pe.wait_ge(A["pcopied"], NTURN[kind] * it + last + 1)
                    if a >= 2:
                        pe.wait_ge(A["orow"], 2 * NA * it + ocopy_step(a - 2))
                    kb = kblocks(kind, a)
                    for e, (c, kr) in enumerate(kb):
                        if t < PT:
                            v = B["vtok"][0:kr, e, HD * j:HD * (j + 1)]
                        elif kind == "mem" or e == 0:
                            v = B["cv"][0:kr, e, HD * j:HD * (j + 1)]
                        else:
                            v = B["vtok"][0:kr, PT, HD * j:HD * (j + 1)]
                        mm = pe.matmul(bank(6 + j, HD, rows), B["pT"][0:kr, a % 2, c:c + rows], v,
                                       start=(e == 0), stop=(e == len(kb) - 1))
                    mm.then_inc(A["pv"], 1)

                def turn_o(t):
                    n = TURN[kind]["o", t, 0]
                    rows = TILES[t][1]
                    pe.wait_ge(A["orow"], 2 * NA * it + ocopy_step(2 * t + 1))
                    free_turn_bank(n)
                    b = 512 * (4 + n % 2)
                    pe.transpose(PS[:, b:b + rows], B["osb"][0:rows, t % 2, :], ident[0:rows, 0:rows])\
                      .then_inc(A["pturned"], 1)

                pe.wait_ge(A["nrm"], NRM[kind] * it + NRM[kind])
                pe.wait_ge(A["cloaded"], (64 if kind == "fox" else 32) * (it + 1))
                for q in range(NTT[kind]):
                    if q in TTV[kind]:
                        break
                    turn_tokens(q)
                pe.wait_ge(A["vcopied"], NV[kind] * it + NV[kind])
                scores(0)
                for q in TTV[kind]:
                    turn_tokens(q)
                scores(1)
                turn_probs(0)
                pe.wait_ge(A["tcopied"], NTT[kind] * it + NTT[kind])
                for a in range(NA):
                    if a + 2 < NA:
                        scores(a + 2)
                    if a + 1 < NA:
                        turn_probs(a + 1)
                    weigh(a)
                    if a % 2 == 0 and a >= 2:
                        turn_o(a // 2 - 1)
                turn_o(NT - 1)
                out_product(kind, it, (6, 12, 18))

            pe.wait_ge(LOOPS["conv"]["resid"], 24 * ITER["conv"] + 4)
            pe.wait_ge(s_smallc, 4)
            with repeated(pe, ITER["fox"]) as it:
                pair_step("fox", it)

            pe.wait_ge(mp["scaled"], 2)
            pe.wait_ge(LOOPS["fox"]["resid"], 24 * ITER["fox"] + 4)
            for k in range(KT):
                for t in range(2):
                    mm = pe.transpose(PS[:, 512 * k + t * P:512 * k + (t + 1) * P],
                                      memtok[:, t, k * P:(k + 1) * P], ident[:, :])
                mm.then_inc(mp["turned"], 1)
            pe.wait_ge(mp["split"], 4)
            with repeated(pe, ITER["mem"]) as it:
                pair_step("mem", it)

            pe.wait_ge(LOOPS["mem"]["resid"], 24 * ITER["mem"] + 4)
            norm_mean(2, 0)
            ffn(1)
            for t in range(NT):
                s, n = TILES[t]
                pe.wait_ge(FFN[1]["resid"], 24 * (NF - 1) + 8 * (t // 3 + 1) + 4)
                if t == 0:
                    pe.wait_ge(FFN[1]["act_made"], 6 * NF + 2)
                if t >= 2:
                    pe.wait_ge(fin["dve"], 6 * (t - 1))
                for k in range(KT):
                    b = 512 * (2 * (t % 2) + k // 4) + P * (k % 4)
                    mm = pe.transpose(PS[0:n, b:b + P], xT[:, k, s:s + n], ident[:, :])
                    if k % 4 == 3:
                        mm.then_inc(fin["turned"], 1)


_OUTS = ["y_prompt", "y_sample", "fox_k_prompt", "fox_v_prompt", "fox_logf_prompt", "conv_state_prompt",
         "mem_k_prompt", "mem_v_prompt", "fox_k_sample", "fox_v_sample", "fox_logf_sample", "conv_state_sample"]


def kernel(**inputs):
    import numpy as np
    import concourse.bacc as bacc
    from concourse.bass_utils import run_bass_kernel_spmd

    nc = bacc.Bacc("TRN2", target_bir_lowering=False, num_devices=1, dynamic_dma_scratch_size=64)
    arrays, ins = {}, {}
    for name, a in inputs.items():
        a = np.ascontiguousarray(a)
        arrays[f"in_{name}"] = a
        ins[name] = nc.dram_tensor(f"in_{name}", a.shape, mybir.dt.from_np(a.dtype), kind="ExternalInput").ap()
    depth, dec_b = inputs["cache_fox_k"].shape[0:2]
    b, seq = inputs["x_prompt"].shape[0:2]
    dec = inputs["x_sample"].shape[1]
    fh, hd = inputs["cache_fox_k"].shape[3:5]
    nmem, mh = inputs["cache_mem_k"].shape[2:4]
    ck, cc = inputs["state_conv"].shape[2:4]
    shapes = [inputs["x_prompt"].shape, inputs["x_sample"].shape, (depth, b, seq, fh, hd), (depth, b, seq, fh, hd),
              (depth, b, seq, fh), (depth, b, ck, cc), (depth, b, nmem, mh, hd), (depth, b, nmem, mh, hd),
              (depth, dec_b, dec, fh, hd), (depth, dec_b, dec, fh, hd), (depth, dec_b, dec, fh),
              (depth, dec_b, ck, cc)]
    outs = {n: nc.dram_tensor(f"out_{n}", s, F32, kind="ExternalOutput").ap() for n, s in zip(_OUTS, shapes)}
    hybrid_step(nc, ins, outs)
    r = run_bass_kernel_spmd(nc, [arrays], core_ids=[0])
    return tuple(r.results[0][f"out_{n}"] for n in _OUTS)
```
